# Optimizing a Trainium2 kernel written in Bass

```python
import jax, jax.numpy as jnp
from jax import lax
import numpy as np

D_MODEL = 2048
BATCH = 1
SEQ = 512
DEPTH = 1

CHUNK = 64
N_MIXERS = 2
HEAD_DIM = 128
N_HEADS = D_MODEL // HEAD_DIM
Q_BLOCK = 128
POOL_WINDOWS = (2, 4, 8, 16)
N_POOL_GROUPS = len(POOL_WINDOWS)
POOL_GROUP = D_MODEL // N_POOL_GROUPS
D_FF = -(-8 * D_MODEL // (3 * 256)) * 256
N_FOX_LAYERS = (DEPTH + N_MIXERS - 1) // N_MIXERS
N_POOL_LAYERS = DEPTH // N_MIXERS
RMS_EPS = 1e-6
NEG_INF = -1e30

kernel_name = "fox_pool_hybrid_encoder"

def rmsnorm(x, g):
    xf = x.astype(jnp.float32)
    y = xf * lax.rsqrt(jnp.mean(xf * xf, axis=-1, keepdims=True) + RMS_EPS)
    return (y * g.astype(jnp.float32)).astype(x.dtype)

def forgetting_attention(h, w_in, b_f, g_q, g_k, w_out):
    B, S, D = h.shape
    proj = jnp.einsum('bsd,de->bse', h, w_in)
    q = proj[..., :D].reshape(B, S, N_HEADS, HEAD_DIM)
    k = proj[..., D:2 * D].reshape(B, S, N_HEADS, HEAD_DIM)
    v = proj[..., 2 * D:3 * D].reshape(B, S, N_HEADS, HEAD_DIM)
    f_logit = proj[..., 3 * D:]
    q = rmsnorm(q, g_q)
    k = rmsnorm(k, g_k)
    log_f = jax.nn.log_sigmoid((f_logit + b_f).astype(jnp.float32))
    c = jnp.cumsum(log_f, axis=1).transpose(0, 2, 1)
    nb = S // Q_BLOCK
    q_blocks = q.reshape(B, nb, Q_BLOCK, N_HEADS, HEAD_DIM).transpose(1, 0, 2, 3, 4)
    c_blocks = c.reshape(B, N_HEADS, nb, Q_BLOCK).transpose(2, 0, 1, 3)
    starts = jnp.arange(nb) * Q_BLOCK
    k_pos = jnp.arange(S)
    scale = HEAD_DIM ** -0.5

    def block(args):
        qb, cb, start = args
        s = jnp.einsum('bqhd,bkhd->bhqk', qb, k).astype(jnp.float32) * scale
        s = s + (cb[..., :, None] - c[..., None, :])
        q_pos = start + jnp.arange(Q_BLOCK)
        s = jnp.where(q_pos[:, None] >= k_pos[None, :], s, NEG_INF)
        p = jax.nn.softmax(s, axis=-1).astype(v.dtype)
        return jnp.einsum('bhqk,bkhd->bqhd', p, v)

    o = lax.map(block, (q_blocks, c_blocks, starts))
    o = o.transpose(1, 0, 2, 3, 4).reshape(B, S, D)
    return jnp.einsum('bsd,de->bse', o, w_out)

def multiscale_pool(h, w, b, scale):
    B, S, D = h.shape
    hf = h.astype(jnp.float32)
    cs = jnp.concatenate([jnp.zeros((B, 1, D), jnp.float32), jnp.cumsum(hf, axis=1)], axis=1)
    t = jnp.arange(S)
    means = []
    for g, win in enumerate(POOL_WINDOWS):
        csg = cs[..., g * POOL_GROUP:(g + 1) * POOL_GROUP]
        lo = jnp.maximum(t + 1 - win, 0)
        cnt = (t + 1 - lo).astype(jnp.float32)
        means.append((csg[:, t + 1] - csg[:, lo]) / cnt[None, :, None])
    y = (jnp.concatenate(means, axis=-1) - hf).astype(h.dtype)
    y = jnp.einsum('bsgc,gce->bsge', y.reshape(B, S, N_POOL_GROUPS, POOL_GROUP), w).reshape(B, S, D)
    return (y + b) * scale

def swiglu(h, w_gu, w_down):
    gu = jnp.einsum('bsd,df->bsf', h, w_gu)
    gate, up = gu[..., :D_FF], gu[..., D_FF:]
    return jnp.einsum('bsf,fd->bsd', jax.nn.silu(gate) * up, w_down)

def setup_inputs(seed: int = 0) -> dict:
    key = jax.random.key(seed)
    ks = jax.random.split(key, 13)
    f32 = jnp.float32
    D = D_MODEL
    x = jax.random.normal(ks[0], (BATCH, SEQ, D), f32)
    mix_norm_g = 1.0 + 0.02 * jax.random.normal(ks[1], (DEPTH, D), f32)
    ffn_norm_g = 1.0 + 0.02 * jax.random.normal(ks[2], (DEPTH, D), f32)
    fox_w_in = jax.random.normal(ks[3], (N_FOX_LAYERS, D, 3 * D + N_HEADS), f32) * D ** -0.5
    fox_b_f = 2.0 + 0.5 * jax.random.normal(ks[4], (N_FOX_LAYERS, N_HEADS), f32)
    fox_q_norm_g = 1.0 + 0.02 * jax.random.normal(ks[5], (N_FOX_LAYERS, HEAD_DIM), f32)
    fox_k_norm_g = 1.0 + 0.02 * jax.random.normal(ks[6], (N_FOX_LAYERS, HEAD_DIM), f32)
    fox_w_out = jax.random.normal(ks[7], (N_FOX_LAYERS, D, D), f32) * D ** -0.5
    pool_w = jax.random.normal(ks[8], (N_POOL_LAYERS, N_POOL_GROUPS, POOL_GROUP, POOL_GROUP), f32) * POOL_GROUP ** -0.5
    pool_b = 0.01 * jax.random.normal(ks[9], (N_POOL_LAYERS, D), f32)
    pool_scale = 1.0 + 0.02 * jax.random.normal(ks[10], (N_POOL_LAYERS, D), f32)
    ffn_w_gate_up = jax.random.normal(ks[11], (DEPTH, D, 2 * D_FF), f32) * D ** -0.5
    ffn_w_down = jax.random.normal(ks[12], (DEPTH, D_FF, D), f32) * D_FF ** -0.5
    return {"x": x, "mix_norm_g": mix_norm_g, "ffn_norm_g": ffn_norm_g,
            "fox_w_in": fox_w_in, "fox_b_f": fox_b_f, "fox_q_norm_g": fox_q_norm_g,
            "fox_k_norm_g": fox_k_norm_g, "fox_w_out": fox_w_out,
            "pool_w": pool_w, "pool_b": pool_b, "pool_scale": pool_scale,
            "ffn_w_gate_up": ffn_w_gate_up, "ffn_w_down": ffn_w_down}

def reference(x, mix_norm_g, ffn_norm_g, fox_w_in, fox_b_f, fox_q_norm_g, fox_k_norm_g,
              fox_w_out, pool_w, pool_b, pool_scale, ffn_w_gate_up, ffn_w_down):
    for i in range(DEPTH):
        j = i // N_MIXERS
        h = rmsnorm(x, mix_norm_g[i])
        if i % N_MIXERS == 0:
            x = x + forgetting_attention(h, fox_w_in[j], fox_b_f[j], fox_q_norm_g[j],
                                         fox_k_norm_g[j], fox_w_out[j])
        else:
            x = x + multiscale_pool(h, pool_w[j], pool_b[j], pool_scale[j])
        h = rmsnorm(x, ffn_norm_g[i])
        x = x + swiglu(h, ffn_w_gate_up[i], ffn_w_down[i])
    return x


_drawn_inputs = setup_inputs


def setup_inputs(seed=0):
    import zlib

    import numpy as np

    out = dict(_drawn_inputs(seed))
    spreads = {}
    factors = {'mix_norm_g': 4.2, 'ffn_norm_g': 4.006, 'fox_q_norm_g': 7.391, 'fox_k_norm_g': 8.0}
    for name, (base, spread) in spreads.items():
        noise = np.random.default_rng([zlib.crc32(name.encode()), seed]).standard_normal(out[name].shape)
        drawn = base * np.exp(spread * noise) if base else spread * noise
        out[name] = __import__('jax').numpy.asarray(drawn.astype(out[name].dtype))
    for name, factor in factors.items():
        out[name] = (out[name] * factor).astype(out[name].dtype)
    return out
```

```python
from contextlib import ExitStack

import numpy as np

import concourse.bass as bass
from concourse import mybir

P = 128
F32 = mybir.dt.float32
F32R = mybir.dt.float32r
ALU = mybir.AluOpType
ACT = mybir.ActivationFunctionType
AX = mybir.AxisListType
EPS = 1e-6
NEG_INF = -1e30
BIG = 3.0e38


def encoder_layer(nc, x, mix_g, ffn_g, w_in, b_f, g_q, g_k, w_out, w_gu, w_down, y):
    S, D = x.shape
    NH = b_f.shape[1]
    HD = g_q.shape[1]
    FF = w_down.shape[0]
    NT = S // P
    KU = 4
    KG = D // (KU * P)
    NK = D // P
    CW = 512
    ND = D // CW
    NP = FF // CW
    QKV = 3 * HD
    assert NT == 4 and KG == 4 and ND == 4 and HD == P and S == CW and NH == 16 and FF % CW == 0
    U_OUT = KG * NH
    U_FFN = U_OUT + KG * ND
    U_LOOP = U_FFN + 8
    U_END = U_LOOP + 12 * (NP - 1)
    B_OUT, B_FFN = 4 * NH, 4 * NH + 4 * ND
    B_LOOP = B_FFN + 8
    B_END = B_LOOP + 24 * (NP - 1)
    OFF = [0, 128, 384, 768]
    SW = 1280

    dram_c = nc.dram_tensor("c_scratch", (NH, S), F32, kind="Internal").ap()

    ctx = ExitStack()
    with ctx:
        def sb(name, shape, dt=F32):
            return ctx.enter_context(nc.sbuf_tensor(name, shape, dt))

        def sem(name):
            return ctx.enter_context(nc.semaphore(name))

        act_hi = sb("act_hi", [P, NK, S], F32R)
        act_lo = sb("act_lo", [P, NK, S], F32R)
        rows = sb("rows", [P, ND, NT, CW])
        w_raw = sb("w_raw", [P, 2, KU, CW])
        w_hi = sb("w_hi", [P, 2, KU, CW], F32R)
        w_lo = sb("w_lo", [P, 2, KU, CW], F32R)
        work_r = sb("work_r", [P, 11 * 512], F32R)
        qT_hi, kT_hi = work_r[:, 0:512], work_r[:, 512:1024]
        qT_lo, kT_lo = work_r[:, 1024:1536], work_r[:, 1536:2048]
        v_hi = work_r[:, 2048:2560].rearrange("p (t c) -> p t c", t=NT)
        v_lo = work_r[:, 2560:3072].rearrange("p (t c) -> p t c", t=NT)
        pT_hi, pT_lo = work_r[:, 3072:3072 + SW], work_r[:, 4352:4352 + SW]
        hid_hi = work_r[:, 0:2048].rearrange("p (k c) -> p k c", k=KU)
        hid_lo = work_r[:, 2048:4096].rearrange("p (k c) -> p k c", k=KU)
        diag_hi = work_r[:, 4096:4608].rearrange("p (t c) -> p t c", t=NT)
        diag_lo = work_r[:, 4608:5120].rearrange("p (t c) -> p t c", t=NT)
        work = sb("work", [P, 2 * SW])
        prob, bias_t = work[:, 0:SW], work[:, SW:2 * SW]
        silu_t = work[:, 0:2048].rearrange("p (k c) -> p k c", k=KU)
        qk_raw = sb("qk_raw", [P, NT, 2 * HD])
        hid_raw = qk_raw[:].rearrange("p t c -> p (t c)").rearrange("p (b c) -> p b c", b=2)
        c_key = sb("c_key", [P, S])
        rms2_b = sb("rms2_b", [P, S])
        junk_act = sb("junk_act", [P, 2, CW])
        junk_dve = sb("junk_dve", [P, 2, HD])
        ident = sb("ident", [P, P])
        causal = sb("causal", [P, S])
        causal_r = sb("causal_r", [P, S], F32R)
        gain_rows = sb("gain_rows", [2 * NK + 2, P])
        gain = sb("gain", [P, 2 * NK + 2])
        gain_q = sb("gain_q", [P, 1])
        wf_raw = sb("wf_raw", [P, NK, NH])
        b_f_all = sb("b_f_all", [P, NH])
        ss_x = sb("ss_x", [P, NT, ND])
        ss_sum = sb("ss_sum", [P, NT])
        rms_x = sb("rms_x", [P, NT])
        rms_sq = sb("rms_sq", [P, NT])
        mean_t = sb("mean_t", [P, NT])
        neg_half = sb("neg_half", [P, NT])
        ss_qk = sb("ss_qk", [P, NT, 2])
        mean_qk = sb("mean_qk", [P, NT, 2])
        inv_qk = sb("inv_qk", [P, NT, 2])
        fac_qk = sb("fac_qk", [P, NT, 2])
        z = sb("z", [P, NT, NH])
        z_abs = sb("z_abs", [P, NT, NH])
        z_log = sb("z_log", [P, NT, NH])
        logf = sb("logf", [P, NT, NH])
        logf_hi = sb("logf_hi", [P, NT, NH], F32R)
        logf_lo = sb("logf_lo", [P, NT, NH], F32R)
        c_rows = sb("c_rows", [NH, S])
        c_cols = sb("c_cols", [P, NT, NH])
        c_query = sb("c_query", [P, NT])
        neg_max = sb("neg_max", [P, NT])
        p_sum = sb("p_sum", [P, NT])
        p_inv = sb("p_inv", [P, NT])
        G = [ctx.enter_context(nc.psum_tensor(f"gemm{i}", [P, CW], F32)) for i in range(4)]
        X = [ctx.enter_context(nc.psum_tensor(f"aux{i}", [P, CW], F32)) for i in range(4)]

        x_ld = [sem(f"x_loaded{d}") for d in range(ND)]
        gain_ld, wf_ld, bf_ld = sem("gain_loaded"), sem("wf_loaded"), sem("b_f_loaded")
        w_ld = [sem("w_loaded0"), sem("w_loaded1")]
        w_hi_done, w_lo_done = sem("w_hi_done"), sem("w_lo_done")
        slot_done = sem("slot_done")
        bank_free = sem("bank_free")
        consts = sem("consts")
        consts_step = sem("consts_step")
        causal_done = sem("causal_done")
        gain_T, gain_done, gain_q_done = sem("gain_T"), sem("gain_done"), sem("gain_q_done")
        tr_done, tr_hi, tr_lo = sem("tr_done"), sem("tr_hi"), sem("tr_lo")
        ssx_done, sum_done, rms_done, rms_step = (sem("ssx_done"), sem("sum_done"),
                                                  sem("rms_done"), sem("rms_step"))
        evac_act = sem("evac_act")
        ssqk_done, fac_step, fac_done, qk_norm = (sem("ssqk_done"), sem("fac_step"),
                                                  sem("fac_done"), sem("qk_norm"))
        qk_tr, qk_hi, qk_lo = sem("qk_tr"), sem("qk_hi"), sem("qk_lo")
        score_done, max_done, exp_done = sem("score_done"), sem("max_done"), sem("exp_done")
        inv_done, prob_done = sem("inv_done"), sem("prob_done")
        pT_done, pT_hi_done, pT_lo_done = sem("pT_done"), sem("pT_hi_done"), sem("pT_lo_done")
        o_done, o_read = sem("o_done"), sem("o_read")
        z_done, zabs_done, zexp_done, zlog_done = (sem("z_done"), sem("zabs_done"),
                                                   sem("zexp_done"), sem("zlog_done"))
        logf_done, logf_hi_done, logf_split = sem("logf_done"), sem("logf_hi_done"), sem("logf_split")
        c_done, crow_read, ccol_read = sem("c_done"), sem("crow_read"), sem("ccol_read")
        c_stored, ckey_ld = sem("c_stored"), sem("ckey_loaded")
        bias_step, bias_done = sem("bias_step"), sem("bias_done")
        oT_hi_done, oT_lo_done = sem("oT_hi_done"), sem("oT_lo_done")
        diag_hi_done, diag_done, rms2_mm, rms2_done = (sem("diag_hi_done"), sem("diag_done"),
                                                       sem("rms2_mm"), sem("rms2_done"))
        silu_done, silu_scaled = sem("silu_done"), sem("silu_scaled")
        hid_hi_done, hid_lo_done = sem("hid_hi_done"), sem("hid_lo_done")
        y_stored = sem("y_stored")
        waited = sem("waited")

        f32 = lambda ap: ap.bitcast(F32)
        x_cols = x.rearrange("(t p) (d c) -> d p t c", p=P, c=CW)
        y_cols = y.rearrange("(t p) (d c) -> d p t c", p=P, c=CW)

        rows_flat = rows[:].rearrange("p d t c -> p (d t c)")

        def landed(pair, j, in_proj):
            n = pair + j // 2 + 1
            return 48 * n if in_proj else 16 * n + 32 * (U_OUT // 2)

        def fixed(n):
            return isinstance(n, int)

        block = ctx.enter_context(nc.Block())

        @block.sync
        def _(sp):
            def load(pair, j, dst, src):
                if not (fixed(pair) and 2 * pair + j < 2):
                    sp.wait_ge(w_lo_done, 2 * (2 * pair + j - 1))
                sp.dma_start(dst, src).then_inc(w_ld[j % 2], 16)

            w_in_v = w_in[:, 0:3 * D].rearrange("(g k p) (s c) -> g p k s c", k=KU, p=P, c=D)
            w_out_v = w_out.rearrange("(g k p) (d c) -> d g p k c", k=KU, p=P, c=CW)
            w_gu_v = w_gu.rearrange("(g k p) c -> g p k c", k=KU, p=P)
            w_down_v = w_down.rearrange("(r k p) (d c) -> r d p k c", k=KU, p=P, c=CW)

            def load_in(h, kg):
                for s in range(3):
                    load(2 * h, kg, w_raw[:, kg % 2, :, s * HD:(s + 1) * HD],
                         w_in_v[kg, :, :, s, bass.ts(h, HD)])

            def load_c(h):
                if not (fixed(h) and h == 0):
                    sp.wait_ge(bias_done, h)
                sp.dma_start(c_key[:], dram_c[bass.ds(h, 1), :].broadcast_to((P, S)))\
                    .then_inc(ckey_ld, 16)

            for d in range(ND):
                sp.dma_start(rows[:, d], x_cols[d]).then_inc(x_ld[d], 16)
                if d == 0:
                    sp.dma_start(wf_raw[:], w_in[:, 3 * D:3 * D + NH].rearrange("(k p) c -> p k c", p=P))\
                        .then_inc(wf_ld, 16)
                if d < 2:
                    load_in(0, d)
            load_in(0, 2)
            load_in(0, 3)
            for kg in range(KG):
                load_in(1, kg)
            sp.wait_ge(crow_read, 1)
            sp.dma_start(dram_c, c_rows[:]).then_inc(c_stored, 16)
            sp.wait_ge(c_stored, 16)
            load_c(0)
            load_c(1)
            with sp.Fori(2, NH) as h:
                load_in(h, 0)
                load_c(h)
                for kg in range(1, KG):
                    load_in(h, kg)
            for d in range(ND):
                for kg in range(KG):
                    load(U_OUT // 2, KG * d + kg, w_raw[:, kg % 2], w_out_v[d, kg])
                    if d == 0:
                        sp.wait_ge(oT_lo_done, 2 * kg + 2)
                        sp.dma_start(rows[:, kg], x_cols[kg]).then_inc(x_ld[kg], 16)

            def load_gate_up(pair, j0, p, first_col):
                for kg in range(KG):
                    load(pair, j0 + kg, w_raw[:, kg % 2], w_gu_v[kg][:, :, bass.ds(p * CW + first_col, CW)])

            load_gate_up(U_FFN // 2, 0, 0, 0)
            load_gate_up(U_FFN // 2, 4, 0, FF)
            with sp.Fori(1, NP) as p:
                pair = 6 * (p - 1) + U_LOOP // 2
                load_gate_up(pair, 0, p, 0)
                for d in range(ND):
                    src = w_down_v[bass.ds(p - 1, 1), d].rearrange("r p k c -> (r p) k c")
                    load(pair, 4 + d, w_raw[:, d % 2], src)
                load_gate_up(pair, 8, p, FF)
            for d in range(ND):
                load(U_END // 2, d, w_raw[:, d % 2], w_down_v[NP - 1, d])
            for d in range(ND - 1):
                sp.wait_ge(bank_free, B_END + 4 * d + 4)
                sp.dma_start(y_cols[d], rows[:, d]).then_inc(y_stored, 16)
            for t in range(NT):
                sp.wait_ge(bank_free, B_END + 4 * (ND - 1) + t + 1)
                sp.dma_start(y_cols[ND - 1][:, t], rows[:, ND - 1, t]).then_inc(y_stored, 16)
            sp.wait_ge(y_stored, 16 * (ND - 1 + NT))

        def on_its_own(engine):
            engine.sem_inc(waited, 1)

        @block.gpsimd
        def _(pool):
            g = nc.gpsimd
            g.memset(ident[:], 0.0).then_inc(consts_step, 1)
            g.memset(causal[:], 1.0).then_inc(consts_step, 1)
            g.memset(neg_half[:], -0.5)
            pool.wait_ge(consts_step, 2)
            g.affine_select(out=ident[:], in_=ident[:], compare_op=ALU.not_equal, fill=1.0, base=0,
                            pattern=[[-1, P]], channel_multiplier=1).then_inc(consts, 1)
            g.affine_select(out=causal[:], in_=causal[:], compare_op=ALU.is_ge, fill=0.0, base=0,
                            pattern=[[1, S]], channel_multiplier=-1).then_inc(consts, 1)

            def inv_rms(nth, steps, signals):
                pool.wait_ge(sum_done, nth)
                g.tensor_scalar(mean_t[:], ss_sum[:], 1.0 / D, EPS, ALU.mult, ALU.add)\
                    .then_inc(rms_step, 1)
                pool.wait_ge(rms_step, steps + 1)
                g.tensor_tensor(rms_x[:], mean_t[:], neg_half[:], ALU.pow).then_inc(signals, 1)

            def factors(h, t):
                n = NT * h + t
                pool.wait_ge(ssqk_done, n + 1)
                on_its_own(pool)
                g.tensor_scalar(mean_qk[:, t], ss_qk[:, t], rms_sq[:, t:t + 1], EPS,
                                ALU.mult, ALU.add).then_inc(fac_step, 1)
                pool.wait_ge(fac_step, 2 * n + 1)
                on_its_own(pool)
                g.tensor_tensor(inv_qk[:, t], mean_qk[:, t], neg_half[:, 0:2], ALU.pow)\
                    .then_inc(fac_step, 1)
                pool.wait_ge(fac_step, 2 * n + 2)
                on_its_own(pool)
                g.tensor_scalar(fac_qk[:, t], inv_qk[:, t], rms_x[:, t:t + 1], None, ALU.mult)\
                    .then_inc(fac_done, 1)

            def bias(h):
                if not (fixed(h) and h == 0):
                    pool.wait_ge(max_done, NT * h)
                pool.wait_ge(ckey_ld, 16 * (h + 1))
                on_its_own(pool)
                g.tensor_copy(c_query[:], c_cols[:, :, bass.ds(h, 1)].rearrange("p t o -> p (t o)"))\
                    .then_inc(bias_step, 1)
                pool.wait_ge(bias_step, 2 * h + 1)
                on_its_own(pool)
                for i in range(NT):
                    last = g.tensor_scalar(bias_t[:, OFF[i]:OFF[i] + P * (i + 1)],
                                           c_key[:, 0:P * (i + 1)], -1.0, c_query[:, i:i + 1],
                                           ALU.mult, ALU.add)
                last.then_inc(bias_step, 1)
                pool.wait_ge(bias_step, 2 * h + 2)
                on_its_own(pool)
                for i in range(NT):
                    dg = bias_t[:, OFF[i] + P * i:OFF[i] + P * (i + 1)]
                    last = g.affine_select(out=dg, in_=dg, compare_op=ALU.is_ge, fill=NEG_INF, base=0,
                                           pattern=[[-1, P]], channel_multiplier=1)
                last.then_inc(bias_done, 1)

            inv_rms(1, 0, signals=rms_step)
            pool.wait_ge(rms_step, 2)
            g.tensor_tensor(mean_t[:], rms_x[:], rms_x[:], ALU.mult).then_inc(rms_step, 1)
            pool.wait_ge(rms_step, 3)
            g.tensor_scalar(rms_sq[:], mean_t[:], 1.0 / HD, None, ALU.mult).then_inc(rms_done, 1)
            pool.wait_ge(rms_done, 1)
            for t in range(3):
                factors(0, t)
            factors(0, 3)
            pool.wait_ge(ccol_read, 1)
            bias(0)
            bias(1)
            for t in range(3):
                factors(1, t)
            with pool.Fori(2, NH) as h:
                factors(h - 1, 3)
                bias(h)
                for t in range(3):
                    factors(h, t)
            factors(NH - 1, 3)
            inv_rms(2, 3, signals=rms_done)
            pool.wait_ge(rms2_done, 1)

            def scale_silu(p, j):
                pool.wait_ge(silu_done, 4 * p + j + 1)
                g.tensor_tensor(silu_t[:, j], silu_t[:, j], rms2_b[:], ALU.mult).then_inc(silu_scaled, 1)

            with pool.Fori(0, NP) as p:
                for j in range(4):
                    scale_silu(p, j)

        @block.tensor
        def _(pe):
            mm = nc.tensor.matmul

            def three(out, a_hi, a_lo, b_hi, b_lo, first, last):
                mm(out, a_hi, b_hi, start=first, stop=False)
                mm(out, a_hi, b_lo, start=False, stop=False)
                return mm(out, a_lo, b_hi, start=False, stop=last)

            def wait_unit(pair, j):
                pe.wait_ge(w_lo_done, 2 * (2 * pair + j) + 2)

            def rows_slot(bank, j, k0, t, first, last, width=CW, src_hi=act_hi, src_lo=act_lo,
                          ks=range(KU), split=None):
                for k in ks:
                    if split:
                        split(k)
                    i = three(bank[:, 0:width],
                              src_hi[:, k0 + k, bass.ts(t, P)], src_lo[:, k0 + k, bass.ts(t, P)],
                              w_hi[:, j % 2, k, 0:width], w_lo[:, j % 2, k, 0:width],
                              first and k == 0, last and k == KU - 1)
                if KU - 1 in ks:
                    i.then_inc(slot_done, 1)

            def cols_slot(bank, j, k0, f, first, last):
                for k in range(KU):
                    i = three(bank[:, :],
                              w_hi[:, j % 2, k, bass.ts(f, P)], w_lo[:, j % 2, k, bass.ts(f, P)],
                              act_hi[:, k0 + k, :], act_lo[:, k0 + k, :],
                              first and k == 0, last and k == KU - 1)
                i.then_inc(slot_done, 1)

            def transpose_rows(n0, kg):
                for i in range(KU):
                    if n0 + KU * kg + i >= KU:
                        pe.wait_ge(tr_lo, n0 + KU * kg + i - KU + 1)
                    for t in range(NT):
                        last = nc.tensor.transpose(X[i][:, bass.ts(t, P)], rows[:, kg, t, bass.ts(i, P)],
                                                   ident[:])
                    last.then_inc(tr_done, 1)

            def qk_transpose(h, t):
                if t == 0 and not (fixed(h) and h == 0):
                    pe.wait_ge(o_read, h)
                pe.wait_ge(qk_norm, NT * h + t + 1)
                nc.tensor.transpose(X[0][:, bass.ts(t, P)], qk_raw[:, t, 0:HD], ident[:])
                i = nc.tensor.transpose(X[1][:, bass.ts(t, P)], qk_raw[:, t, HD:2 * HD], ident[:])
                if t == NT - 1:
                    i.then_inc(qk_tr, 1)

            def scores(h):
                pe.wait_ge(qk_lo, 2 * h + 2)
                dst = [X[2][:, 0:128], X[2][:, 128:384], X[3][:, 0:384], X[0][:, 0:512]]
                for i in range(NT):
                    n = P * (i + 1)
                    last = three(dst[i], qT_hi[:, bass.ts(i, P)], qT_lo[:, bass.ts(i, P)],
                                 kT_hi[:, 0:n], kT_lo[:, 0:n], True, True)
                    if i > 0:
                        last.then_inc(score_done, 1)

            def prob_transpose(h):
                pe.wait_ge(prob_done, h + 1)
                for j, dst in enumerate((X[1][:, 0:512], X[2][:, 0:384], X[3][:, 0:256], X[3][:, 256:384])):
                    for i in range(j, NT):
                        last = nc.tensor.transpose(dst[:, bass.ts(i - j, P)],
                                                   prob[:, OFF[i] + P * j:OFF[i] + P * (j + 1)], ident[:])
                    if j != 2:
                        last.then_inc(pT_done, 1)

            def weighted_v(h):
                pe.wait_ge(pT_lo_done, 3 * h + 3)
                off = [0, 512, 896, 1152]
                for j in range(NT):
                    n = S - P * j
                    i = three(X[0][:, P * j:S], v_hi[:, j], v_lo[:, j],
                              pT_hi[:, off[j]:off[j] + n], pT_lo[:, off[j]:off[j] + n],
                              j == 0, j == NT - 1)
                i.then_inc(o_done, 1)

            ATTN = {0: [("qk", 0), ("qk", 1)], 1: [("qk", 2)], 2: [("qk", 3)], 4: [("scores",)],
                    9: [("prob",)], 11: [("v",)]}
            ATTN_SECOND = {0: [("qk", 0)], 1: [("qk", 1)], 2: [("qk", 2)], 3: [("qk", 3)],
                           5: [("scores",)], 10: [("prob",)], 12: [("v",)]}
            ATTN_LAST = {0: [("qk", 0), ("qk", 1)], 1: [("qk", 2)], 2: [("qk", 3)], 3: [("scores",)],
                         7: [("prob",)], 9: [("v",)]}

            def attention(plan, s, h):
                for piece in plan.get(s, ()):
                    if piece[0] == "qk":
                        qk_transpose(h, piece[1])
                    elif piece[0] == "scores":
                        scores(h)
                    elif piece[0] == "prob":
                        prob_transpose(h)
                    else:
                        weighted_v(h)

            def forget_sums():
                pe.wait_ge(logf_split, 1)
                for j in range(NT):
                    n = S - P * j
                    mm(X[2][0:NH, P * j:S], logf_hi[:, j], causal_r[:, 0:n], start=(j == 0), stop=False)
                    i = mm(X[2][0:NH, P * j:S], logf_lo[:, j], causal_r[:, 0:n],
                           start=False, stop=(j == NT - 1))
                i.then_inc(c_done, 1)
                for q in range(NT):
                    out = X[3][:, q * NH:(q + 1) * NH]
                    for j in range(q + 1):
                        m = causal_r[:, P * (q - j):P * (q - j + 1)]
                        mm(out, m, logf_hi[:, j], start=(j == 0), stop=False)
                        i = mm(out, m, logf_lo[:, j], start=False, stop=(j == q))
                i.then_inc(c_done, 1)

            def first_chunk():
                width = QKV + NH
                for half in range(2):
                    for t in range(NT):
                        if t == 0:
                            pe.wait_ge(w_lo_done, half + 1)
                            pe.wait_ge(tr_lo, 2 * half + 2)
                        rows_slot(G[t], 0, 0, t, True, False, width, ks=(2 * half, 2 * half + 1))
                    if half == 0:
                        pe.wait_ge(x_ld[1], 16)
                        transpose_rows(0, 1)
                for kg in range(1, KG):
                    wait_unit(0, kg)
                    for t in range(NT):
                        rows_slot(G[t], kg, KU * kg, t, False, kg == KG - 1, width,
                                  split=x_split(kg) if t == 0 else None)
                        if t == 1 and kg < KG - 1:
                            pe.wait_ge(x_ld[kg + 1], 16)
                            transpose_rows(0, kg + 1)

            def x_split(kg):
                return lambda k: pe.wait_ge(tr_lo, KU * kg + k + 1)

            def in_chunk(h, second=False):
                for kg in range(KG):
                    wait_unit(2 * h, kg)
                    for t in range(NT):
                        s = KG * kg + t
                        if kg == 0:
                            pe.wait_ge(bank_free, NT * (h - 1) + t + 1)
                        rows_slot(G[t], kg, KU * kg, t, kg == 0, kg == KG - 1, QKV)
                        if second and s == 3:
                            forget_sums()
                        if second and s == 5:
                            pe.wait_ge(crow_read, 1)
                            pe.wait_ge(ccol_read, 1)
                        attention(ATTN_SECOND if second else ATTN, s, h - 1)

            def keep_warm(n):
                for _ in range(n):
                    mm(G[1][:], causal_r[:, 0:P], causal_r[:], start=True, stop=True)

            pe.wait_ge(causal_done, 1)
            pe.wait_ge(consts, 2)
            keep_warm(7)
            pe.wait_ge(x_ld[0], 16)
            transpose_rows(0, 0)
            pe.wait_ge(gain_ld, 16 * 4)
            nc.tensor.transpose(G[0][:, 0:2 * NK + 2], gain_rows[:], ident[0:2 * NK + 2, 0:2 * NK + 2])\
                .then_inc(gain_T, 1)
            keep_warm(8)
            pe.wait_ge(gain_done, 1)
            first_chunk()
            in_chunk(1, second=True)
            with pe.Fori(2, NH) as h:
                in_chunk(h)

            for d in range(ND):
                for kg in range(KG):
                    wait_unit(U_OUT // 2, KG * d + kg)
                    for t in range(NT):
                        s = KG * kg + t
                        if d == 0 and t == 0:
                            pe.wait_ge(oT_lo_done, 2 * kg + 2 if kg < 3 else 9)
                        if kg == 0:
                            pe.wait_ge(bank_free, B_OUT + NT * (d - 1) + t + 1)
                        rows_slot(G[t], kg, KU * kg, t, kg == 0, kg == KG - 1)
                        if d == 0:
                            attention(ATTN_LAST, s, NH - 1)
                        if d == ND - 1 and t == 1 and kg > 0:
                            transpose_rows(NK, kg - 1)

            def ffn_start(s):
                if s == 1:
                    pe.wait_ge(bank_free, B_FFN)
                    transpose_rows(NK, 3)
                if s == 6:
                    pe.wait_ge(diag_done, 1)
                    pe.wait_ge(tr_lo, NK + NK - 3)
                    mm(X[0][:], causal_r[:, P:2 * P], diag_hi.rearrange("p t c -> p (t c)"),
                       start=True, stop=False)
                    mm(X[0][:], causal_r[:, P:2 * P], diag_lo.rearrange("p t c -> p (t c)"),
                       start=False, stop=True).then_inc(rms2_mm, 1)
                if s in (3, 7, 11):
                    pe.wait_ge(tr_lo, NK + KU * (s // 4 + 1) + KU)

            def ffn_chunk(banks, pair, j0, free=None, between=None):
                for kg in range(KG):
                    wait_unit(pair, j0 + kg)
                    for f in range(4):
                        if kg == 0 and free is not None:
                            pe.wait_ge(bank_free, free + f + 1)
                        cols_slot(banks[f], kg, KU * kg, f, kg == 0, kg == KG - 1)
                        if between:
                            between(KG * kg + f)

            def down_chunk(pair, j0, part, free):
                def hidden_split(k):
                    pe.wait_ge(hid_lo_done, 4 * part + k + 1)

                for d in range(ND):
                    wait_unit(pair, j0 + d)
                    for t in range(NT):
                        pe.wait_ge(bank_free, free + 4 * (d - 1) + t + 1)
                        rows_slot(X[t], d, 0, t, True, True, src_hi=hid_hi, src_lo=hid_lo,
                                  split=hidden_split if d == 0 and t == 0 else None)

            pe.wait_ge(tr_lo, NK + KU)
            ffn_chunk(G, U_FFN // 2, 0, B_FFN - 4, ffn_start)
            pe.wait_ge(rms2_done, 1)
            ffn_chunk(X, U_FFN // 2, 4)
            with pe.Fori(1, NP) as p:
                pair = 6 * (p - 1) + U_LOOP // 2
                b0 = 24 * (p - 1) + B_LOOP
                ffn_chunk(G, pair, 0, b0 - 4)
                down_chunk(pair, 4, p - 1, b0 + 4)
                ffn_chunk(X, pair, 8, b0 + 16)
            down_chunk(U_END // 2, 0, NP - 1, B_END)

        @block.scalar
        def _(act):
            a = nc.scalar

            def split_hi(pair, j, half, in_proj=False, first=False):
                width = QKV if in_proj else CW
                if half == 0:
                    act.wait_ge(w_ld[j % 2], landed(pair, j, in_proj))
                    if not (fixed(pair) and 2 * pair + j < 2):
                        act.wait_ge(slot_done, 4 * (2 * pair + j - 1))
                k = slice(2 * half, 2 * half + 2)
                if first:
                    a.activation(w_hi[:, j % 2, k, QKV:QKV + NH],
                                 wf_raw[:, KU * j + 2 * half:KU * j + 2 * half + 2, :], ACT.Copy)
                a.activation(w_hi[:, j % 2, k, 0:width], w_raw[:, j % 2, k, 0:width], ACT.Copy)\
                    .then_inc(w_hi_done, 1)

            for dst, src in ((gain_rows[0:NK, :], mix_g.rearrange("o (k p) -> (o k) p", p=P)),
                             (gain_rows[NK:2 * NK, :], ffn_g.rearrange("o (k p) -> (o k) p", p=P)),
                             (gain_rows[2 * NK:2 * NK + 1, :], g_q),
                             (gain_rows[2 * NK + 1:2 * NK + 2, :], g_k)):
                act.dma_start(dst, src).then_inc(gain_ld, 16)
            act.dma_start(b_f_all[:], b_f.broadcast_to((P, NH))).then_inc(bf_ld, 16)

            def transposed_hi(n, kg, i):
                act.wait_ge(tr_done, n + KU * kg + i + 1)
                a.activation(act_hi[:, KU * kg + i, :], X[i][:], ACT.Copy,
                             scale=gain[:, n + KU * kg + i:n + KU * kg + i + 1]).then_inc(tr_hi, 1)

            def x_squares(d, t):
                if t == 0:
                    act.wait_ge(x_ld[d], 16)
                squares(NT * d + t, d, t)

            def x1_squares(d, t):
                act.wait_ge(bank_free, B_OUT + NT * d + t + 1)
                squares(NT * ND + NT * d + t, d, t)

            def squares(n, d, t):
                if n >= 2:
                    act.wait_ge(ssx_done, n - 1)
                a.activation(junk_act[:, n % 2], rows[:, d, t, :], ACT.Square, accum_out=ss_x[:, t, d:d + 1])\
                    .then_inc(ssx_done, 1)

            def evac(h, t):
                act.wait_ge(slot_done, 4 * (KG * h + KG - 1) + t + 1)
                a.activation(v_hi[:, t], G[t][:, 2 * HD:QKV], ACT.Copy, scale=rms_x[:, t:t + 1])
                a.activation(qk_raw[:, t, :], G[t][:, 0:2 * HD], ACT.Copy).then_inc(evac_act, 1)

            def qk_split(h):
                act.wait_ge(qk_tr, h + 1)
                a.activation(qT_hi, X[0][:], ACT.Copy, scale=gain_q[:]).then_inc(qk_hi, 1)
                a.activation(kT_hi, X[1][:], ACT.Copy, scale=gain[:, 2 * NK + 1:2 * NK + 2])\
                    .then_inc(qk_hi, 1)

            def exps(h):
                for i in range(NT):
                    act.wait_ge(max_done, NT * h + i + 1)
                    pr = prob[:, OFF[i]:OFF[i] + P * (i + 1)]
                    a.activation(pr, pr, ACT.Exp, bias=neg_max[:, i:i + 1], scale=-1.0,
                                 accum_out=p_sum[:, i:i + 1]).then_inc(exp_done, 1)

            def prob_split(h):
                for n, (bank, o, w) in enumerate(((X[1], 0, 512), (X[2], 512, 384), (X[3], 896, 384))):
                    act.wait_ge(pT_done, 3 * h + n + 1)
                    a.activation(pT_hi[:, o:o + w], bank[:, 0:w], ACT.Copy).then_inc(pT_hi_done, 1)

            def out_read(h):
                act.wait_ge(o_done, h + 1)
                a.activation(rows_flat[:, bass.ts(h, S)], X[0][:], ACT.Copy).then_inc(o_read, 1)

            def heads_hi(h0, n, u):
                act.wait_ge(slot_done, 4 * (u + 1))
                act.wait_ge(o_read, h0 + n)
                a.activation(act_hi[:, h0:h0 + n, :].rearrange("p h c -> p (h c)"),
                             rows_flat[:, h0 * S:(h0 + n) * S], ACT.Copy).then_inc(oT_hi_done, 1)

            def in_chunk(h, second=False, last=False):
                for s in range(16):
                    kg = s // 4
                    if s == 0:
                        evac(h - 1, 3)
                        if second:
                            act.wait_ge(zabs_done, 1)
                            a.activation(z_log[:], z_abs[:], ACT.Exp, scale=-1.0).then_inc(zexp_done, 1)
                            act.wait_ge(zexp_done, 1)
                            a.activation(z_abs[:], z_log[:], ACT.Ln, bias=1.0).then_inc(zlog_done, 1)
                    if s % 2 == 0:
                        split_hi(2 * h, kg + 1, s % 4 // 2, in_proj=not (last and kg == 3))
                    if s == 3:
                        if second:
                            act.wait_ge(c_done, 1)
                            a.activation(c_rows[:], X[2][0:NH, :], ACT.Copy).then_inc(crow_read, 1)
                        qk_split(h - 1)
                    if s == 6:
                        exps(h - 1)
                    if s == (11 if second else 10):
                        prob_split(h - 1)
                    if s == (13 if second else 12):
                        out_read(h - 1)
                    if last and s in (6, 9, 13):
                        g = {6: 0, 9: 1, 13: 2}[s]
                        heads_hi(4 * g, 2, KG * h + g)
                        heads_hi(4 * g + 2, 2, KG * h + g)
                    if s >= 13:
                        evac(h, s - 13)

            act.wait_ge(gain_T, 1)
            a.activation(gain[:], G[0][:, 0:2 * NK + 2], ACT.Copy).then_inc(gain_done, 1)
            act.wait_ge(gain_done, 1)
            a.activation(gain_q[:], gain[:, 2 * NK:2 * NK + 1], ACT.Copy, scale=float(HD) ** -0.5)
            for half in range(2):
                transposed_hi(0, 0, 2 * half)
                transposed_hi(0, 0, 2 * half + 1)
                if half == 0:
                    act.wait_ge(wf_ld, 16)
                split_hi(0, 0, half, in_proj=True, first=True)
            for kg in range(KG):
                for half in range(2):
                    split_hi(0, kg + 1, half, in_proj=True, first=kg < KG - 1)
                if kg < KG - 1:
                    for i in range(KU):
                        transposed_hi(0, kg + 1, i)
                for t in range(NT):
                    x_squares(kg, t)
            act.wait_ge(rms_done, 1)
            for t in range(3):
                evac(0, t)
            in_chunk(1, second=True)
            with act.Fori(2, NH - 1) as h:
                in_chunk(h)
            in_chunk(NH - 1, last=True)

            for d in range(ND):
                for s in range(16):
                    if s == 0 and d == 0:
                        evac(NH - 1, 3)
                    if s == 0 and d > 0:
                        x1_squares(d - 1, 3)
                    if s % 2 == 0:
                        split_hi(U_OUT // 2, KG * d + s // 4 + 1, s % 4 // 2)
                    if d == 0:
                        if s == 1:
                            heads_hi(12, 2, U_OUT - 1)
                            heads_hi(14, 1, U_OUT - 1)
                        if s == 2:
                            qk_split(NH - 1)
                        if s == 4:
                            exps(NH - 1)
                        if s == 8:
                            prob_split(NH - 1)
                        if s == 10:
                            act.wait_ge(o_done, NH)
                            a.activation(act_hi[:, NH - 1, :], X[0][:], ACT.Copy).then_inc(oT_hi_done, 1)
                    if d == ND - 1 and s in (6, 10, 14):
                        for i in range(KU):
                            transposed_hi(NK, s // 4 - 1, i)
                    if s >= 13:
                        x1_squares(d, s - 13)

            def silu(p, j, free):
                act.wait_ge(bank_free, free + j + 1)
                a.activation(silu_t[:, j], silu_t[:, j], ACT.Silu).then_inc(silu_done, 1)

            def hidden_hi(j, free):
                act.wait_ge(bank_free, free + j + 1)
                a.activation(hid_hi[:, j], hid_raw[:, j % 2], ACT.Copy).then_inc(hid_hi_done, 1)

            def gate0(s):
                if s == 0:
                    x1_squares(ND - 1, 3)
                if s == 2:
                    for i in range(KU):
                        transposed_hi(NK, 3, i)
                if s == 7:
                    act.wait_ge(rms2_mm, 1)
                    a.activation(rms2_b[:], X[0][:], ACT.Copy).then_inc(rms2_done, 1)
                if s >= 13:
                    silu(0, s - 13, B_FFN)

            def chunk(pair, j0, before):
                for s in range(16):
                    before(s)
                    if s % 2 == 0:
                        split_hi(pair, j0 + s // 4 + 1, s % 4 // 2)

            def up0(s):
                if s == 0:
                    silu(0, 3, B_FFN)
                if s >= 13:
                    hidden_hi(s - 13, B_LOOP - 4)

            chunk(U_FFN // 2, 0, gate0)
            chunk(U_FFN // 2, 4, up0)
            with act.Fori(1, NP) as p:
                pair = 6 * (p - 1) + U_LOOP // 2
                b0 = 24 * (p - 1) + B_LOOP

                def gate(s):
                    if s == 0:
                        hidden_hi(3, b0 - 4)
                    if s >= 13:
                        silu(p, s - 13, b0)

                def down(s):
                    if s == 0:
                        silu(p, 3, b0)

                def up(s):
                    if s >= 13:
                        hidden_hi(s - 13, b0 + 20)

                chunk(pair, 0, gate)
                chunk(pair, 4, down)
                chunk(pair, 8, up)
            hidden_hi(3, B_END - 4)
            for j in range(1, ND):
                for half in range(2):
                    split_hi(U_END // 2, j, half)

        @block.vector
        def _(dve):
            v = nc.vector

            def split_lo(pair, j, half, width=CW, first=False):
                dve.wait_ge(w_hi_done, 2 * (2 * pair + j) + half + 1)
                k = slice(2 * half, 2 * half + 2)
                if first:
                    cols = slice(QKV, QKV + NH)
                    v.tensor_tensor(w_lo[:, j % 2, k, cols],
                                    wf_raw[:, KU * j + 2 * half:KU * j + 2 * half + 2, :],
                                    f32(w_hi[:, j % 2, k, cols]), ALU.subtract)
                v.tensor_tensor(w_lo[:, j % 2, k, 0:width], w_raw[:, j % 2, k, 0:width],
                                f32(w_hi[:, j % 2, k, 0:width]), ALU.subtract).then_inc(w_lo_done, 1)

            def scaled_lo(out, src, scale, hi):
                return v.scalar_tensor_tensor(out, src, scale, f32(hi), ALU.mult, ALU.subtract)

            def transposed_lo(n, kg, i):
                k = KU * kg + i
                dve.wait_ge(tr_hi, n + k + 1)
                scaled_lo(act_lo[:, k, :], X[i][:], gain[:, n + k:n + k + 1], act_hi[:, k, :])\
                    .then_inc(tr_lo, 1)

            def row_sums(n):
                dve.wait_ge(ssx_done, NT * ND * (n + 1))
                v.tensor_reduce(ss_sum[:], ss_x[:], AX.X, ALU.add).then_inc(sum_done, 1)

            def evac(h, t, first=False):
                dve.wait_ge(evac_act, NT * h + t + 1)
                if first:
                    if t == 0:
                        dve.wait_ge(bf_ld, 16)
                    v.scalar_tensor_tensor(z[:, t], G[t][:, QKV:QKV + NH], rms_x[:, t:t + 1], b_f_all[:],
                                           ALU.mult, ALU.add).then_inc(z_done, 1)
                scaled_lo(v_lo[:, t], G[t][:, 2 * HD:QKV], rms_x[:, t:t + 1], v_hi[:, t])\
                    .then_inc(bank_free, 1)
                if not (fixed(h) and NT * h + t == 0):
                    dve.wait_ge(ssqk_done, NT * h + t)
                for s in range(2):
                    qk = qk_raw[:, t, s * HD:(s + 1) * HD]
                    last = v.tensor_tensor_reduce(out=junk_dve[:, s], in0=qk, in1=qk, scale=1.0, scalar=0.0,
                                                  op0=ALU.mult, op1=ALU.add, accum_out=ss_qk[:, t, s:s + 1])
                last.then_inc(ssqk_done, 1)

            def normalise_qk(h, t):
                dve.wait_ge(fac_done, NT * h + t + 1)
                for s in range(2):
                    qk = qk_raw[:, t, s * HD:(s + 1) * HD]
                    last = v.tensor_scalar(qk, qk, fac_qk[:, t, s:s + 1], None, ALU.mult)
                last.then_inc(qk_norm, 1)

            def qk_split(h):
                dve.wait_ge(qk_hi, 2 * h + 1)
                scaled_lo(qT_lo, X[0][:], gain_q[:], qT_hi).then_inc(qk_lo, 1)
                dve.wait_ge(qk_hi, 2 * h + 2)
                scaled_lo(kT_lo, X[1][:], gain[:, 2 * NK + 1:2 * NK + 2], kT_hi).then_inc(qk_lo, 1)

            def biased_scores(h):
                dve.wait_ge(bias_done, h + 1)
                on_its_own(dve)
                src = [X[2][:, 0:128], X[2][:, 128:384], X[3][:, 0:384], X[0][:, 0:512]]
                for i in range(NT):
                    if i != 1:
                        dve.wait_ge(score_done, 3 * h + max(i, 1))
                        on_its_own(dve)
                    c = slice(OFF[i], OFF[i] + P * (i + 1))
                    v.tensor_tensor_reduce(out=prob[:, c], in0=src[i], in1=bias_t[:, c], scale=-1.0,
                                           scalar=BIG, op0=ALU.add, op1=ALU.min,
                                           accum_out=neg_max[:, i:i + 1]).then_inc(max_done, 1)

            def normalise_prob(h):
                dve.wait_ge(exp_done, NT * h + NT)
                v.reciprocal(p_inv[:], p_sum[:]).then_inc(inv_done, 1)
                dve.wait_ge(inv_done, h + 1)
                for i in range(NT):
                    pr = prob[:, OFF[i]:OFF[i] + P * (i + 1)]
                    last = v.tensor_scalar(pr, pr, p_inv[:, i:i + 1], None, ALU.mult)
                last.then_inc(prob_done, 1)

            def prob_split(h):
                for n, (bank, o, w) in enumerate(((X[1], 0, 512), (X[2], 512, 384), (X[3], 896, 384))):
                    dve.wait_ge(pT_hi_done, 3 * h + n + 1)
                    v.tensor_tensor(pT_lo[:, o:o + w], bank[:, 0:w], f32(pT_hi[:, o:o + w]), ALU.subtract)\
                        .then_inc(pT_lo_done, 1)

            heads_split = [0]

            def heads_lo(h0, n):
                heads_split[0] += 1
                dve.wait_ge(oT_hi_done, heads_split[0])
                v.tensor_tensor(act_lo[:, h0:h0 + n, :].rearrange("p h c -> p (h c)"),
                                rows_flat[:, h0 * S:(h0 + n) * S],
                                f32(act_hi[:, h0:h0 + n, :]).rearrange("p h c -> p (h c)"),
                                ALU.subtract).then_inc(oT_lo_done, 1)

            def log_forget():
                dve.wait_ge(z_done, NT)
                v.scalar_tensor_tensor(z_abs[:], z[:], -1.0, z[:], ALU.mult, ALU.max).then_inc(zabs_done, 1)
                dve.wait_ge(zlog_done, 1)
                v.scalar_tensor_tensor(logf[:], z[:], 0.0, z_abs[:], ALU.min, ALU.subtract)\
                    .then_inc(logf_done, 1)
                dve.wait_ge(logf_done, 1)
                v.tensor_copy(logf_hi[:], logf[:]).then_inc(logf_hi_done, 1)
                dve.wait_ge(logf_hi_done, 1)
                v.tensor_tensor(logf_lo[:], logf[:], f32(logf_hi[:]), ALU.subtract).then_inc(logf_split, 1)

            def in_chunk(h, second=False, last=False):
                for s in range(16):
                    kg = s // 4
                    if s == 0:
                        normalise_qk(h - 1, 2)
                        evac(h - 1, 3, first=second)
                        if second:
                            log_forget()
                    if s % 2 == 0:
                        split_lo(2 * h, kg + 1, s % 4 // 2, CW if last and kg == 3 else QKV)
                    if s == 0:
                        normalise_qk(h - 1, 3)
                    if s == 3:
                        if second:
                            dve.wait_ge(c_done, 2)
                            v.tensor_copy(c_cols[:].rearrange("p t h -> p (t h)"), X[3][:, 0:NT * NH])\
                                .then_inc(ccol_read, 1)
                        qk_split(h - 1)
                    if s == (7 if second else 5):
                        biased_scores(h - 1)
                    if s == 8:
                        normalise_prob(h - 1)
                    if s == (11 if second else 10):
                        prob_split(h - 1)
                    if last and s in (6, 9, 13):
                        g = {6: 0, 9: 1, 13: 2}[s]
                        heads_lo(4 * g, 2)
                        heads_lo(4 * g + 2, 2)
                    if s >= 13:
                        evac(h, s - 13)
                    if s >= 14:
                        normalise_qk(h, s - 14)

            dve.wait_ge(consts, 2)
            v.tensor_copy(causal_r[:], causal[:]).then_inc(causal_done, 1)
            for half in range(2):
                transposed_lo(0, 0, 2 * half)
                transposed_lo(0, 0, 2 * half + 1)
                split_lo(0, 0, half, QKV, first=True)
            for kg in range(KG):
                for half in range(2):
                    split_lo(0, kg + 1, half, QKV, first=kg < KG - 1)
                if kg < KG - 1:
                    for i in range(KU):
                        transposed_lo(0, kg + 1, i)
            row_sums(0)
            for t in range(3):
                evac(0, t, first=True)
                if t > 0:
                    normalise_qk(0, t - 1)
            in_chunk(1, second=True)
            with dve.Fori(2, NH - 1) as h:
                in_chunk(h)
            in_chunk(NH - 1, last=True)

            def x1_add(d, t):
                if t == 0:
                    dve.wait_ge(x_ld[d], 32)
                dve.wait_ge(slot_done, 4 * (U_OUT + KG * d + KG - 1) + t + 1)
                v.tensor_tensor(rows[:, d, t, :], G[t][:], rows[:, d, t, :], ALU.add).then_inc(bank_free, 1)

            for d in range(ND):
                for s in range(16):
                    if s == 0 and d == 0:
                        normalise_qk(NH - 1, 2)
                        evac(NH - 1, 3)
                    if s == 0 and d > 0:
                        x1_add(d - 1, 3)
                    if s % 2 == 0:
                        split_lo(U_OUT // 2, KG * d + s // 4 + 1, s % 4 // 2)
                    if d == 0:
                        if s == 0:
                            normalise_qk(NH - 1, 3)
                        if s == 1:
                            heads_lo(12, 2)
                            heads_lo(14, 1)
                        if s == 2:
                            qk_split(NH - 1)
                        if s == 4:
                            biased_scores(NH - 1)
                        if s == 6:
                            normalise_prob(NH - 1)
                        if s == 8:
                            prob_split(NH - 1)
                        if s == 10:
                            dve.wait_ge(oT_hi_done, 9)
                            v.tensor_tensor(act_lo[:, NH - 1, :], X[0][:], f32(act_hi[:, NH - 1, :]),
                                            ALU.subtract).then_inc(oT_lo_done, 1)
                    if d == ND - 1 and s in (6, 10, 14):
                        for i in range(KU):
                            transposed_lo(NK, s // 4 - 1, i)
                    if s >= 13:
                        x1_add(d, s - 13)

            def gate_read(pair, j0, j):
                dve.wait_ge(slot_done, 4 * (2 * pair + j0 + 3) + j + 1)
                v.tensor_tensor(silu_t[:, j], G[j][:], rms2_b[:], ALU.mult).then_inc(bank_free, 1)

            def up_read(pair, j0, p, j):
                if not (fixed(p) and 4 * p + j < 2):
                    dve.wait_ge(hid_lo_done, 4 * p + j - 1)
                dve.wait_ge(silu_scaled, 4 * p + j + 1)
                dve.wait_ge(slot_done, 4 * (2 * pair + j0 + 3) + j + 1)
                v.tensor_tensor(hid_raw[:, j % 2], X[j][:], silu_t[:, j], ALU.mult).then_inc(bank_free, 1)

            def hidden_lo(p, j):
                dve.wait_ge(hid_hi_done, 4 * p + j + 1)
                v.tensor_tensor(hid_lo[:, j], hid_raw[:, j % 2], f32(hid_hi[:, j]), ALU.subtract)\
                    .then_inc(hid_lo_done, 1)

            def down_add(pair, j0, d, t):
                dve.wait_ge(slot_done, 4 * (2 * pair + j0 + d) + t + 1)
                v.tensor_tensor(rows[:, d, t, :], X[t][:], rows[:, d, t, :], ALU.add).then_inc(bank_free, 1)

            def chunk(pair, j0, before):
                for s in range(16):
                    before(s)
                    if s % 2 == 0:
                        split_lo(pair, j0 + s // 4 + 1, s % 4 // 2)

            def gate0(s):
                if s == 0:
                    x1_add(ND - 1, 3)
                if s == 2:
                    for i in range(KU):
                        transposed_lo(NK, 3, i)
                if s == 3:
                    row_sums(1)
                if s == 5:
                    dve.wait_ge(rms_done, 2)
                    for t in range(NT):
                        last = v.tensor_scalar(diag_hi[:, t], ident[:], rms_x[:, t:t + 1], None, ALU.mult)
                    last.then_inc(diag_hi_done, 1)
                    dve.wait_ge(diag_hi_done, 1)
                    for t in range(NT):
                        last = scaled_lo(diag_lo[:, t], ident[:], rms_x[:, t:t + 1], diag_hi[:, t])
                    last.then_inc(diag_done, 1)
                if s == 12:
                    dve.wait_ge(rms2_done, 1)
                if s >= 13:
                    gate_read(U_FFN // 2, 0, s - 13)

            def up0(s):
                if s == 0:
                    gate_read(U_FFN // 2, 0, 3)
                if s >= 13:
                    up_read(U_FFN // 2, 4, 0, s - 13)
                    if s >= 14:
                        hidden_lo(0, s - 14)

            chunk(U_FFN // 2, 0, gate0)
            chunk(U_FFN // 2, 4, up0)
            with dve.Fori(1, NP) as p:
                pair = 6 * (p - 1) + U_LOOP // 2

                def gate(s):
                    if s == 0:
                        up_read(pair, -4, p - 1, 3)
                        hidden_lo(p - 1, 2)
                    if s == 1:
                        hidden_lo(p - 1, 3)
                    if s >= 13:
                        gate_read(pair, 0, s - 13)

                def down(s):
                    if s == 0:
                        gate_read(pair, 0, 3)
                    else:
                        down_add(pair, 4, (s - 1) // 4, (s - 1) % 4)

                def up(s):
                    if s == 0:
                        down_add(pair, 4, 3, 3)
                    if s >= 13:
                        up_read(pair, 8, p, s - 13)
                        if s >= 14:
                            hidden_lo(p, s - 14)

                chunk(pair, 0, gate)
                chunk(pair, 4, down)
                chunk(pair, 8, up)
            up_read(U_END // 2, -4, NP - 1, 3)
            hidden_lo(NP - 1, 2)
            hidden_lo(NP - 1, 3)
            for d in range(ND):
                if d < ND - 1:
                    split_lo(U_END // 2, d + 1, 0)
                    split_lo(U_END // 2, d + 1, 1)
                for t in range(NT):
                    down_add(U_END // 2, 0, d, t)


_INS = ["x", "mix_norm_g", "ffn_norm_g", "fox_w_in", "fox_b_f", "fox_q_norm_g", "fox_k_norm_g",
        "fox_w_out", "ffn_w_gate_up", "ffn_w_down"]


def kernel(**inputs):
    import concourse.bacc as _bacc
    from concourse.bass_utils import run_bass_kernel_spmd as _run

    nc = _bacc.Bacc("TRN2", target_bir_lowering=False, num_devices=1)
    arrays, aps = {}, {}
    for name in _INS:
        a = np.ascontiguousarray(inputs[name])
        if a.ndim == 3:
            a = a[0]
        arrays[f"in_{name}"] = a
        aps[name] = nc.dram_tensor(f"in_{name}", a.shape, mybir.dt.from_np(a.dtype),
                                   kind="ExternalInput").ap()
    shape = arrays["in_x"].shape
    y = nc.dram_tensor("out_y", shape, F32, kind="ExternalOutput").ap()
    encoder_layer(nc, *[aps[n] for n in _INS], y)
    r = _run(nc, [arrays], core_ids=[0])
    return r.results[0]["out_y"].reshape(inputs["x"].shape)
```
